# Optimizing a Trainium2 kernel written in Bass

```python
import math
import jax, jax.numpy as jnp
from jax import lax
import numpy as np

D_MODEL = 1024
BATCH = 1
SEQ = 1024
DEPTH = 1

D_CONV = D_MODEL // 2
D_GLA_V = D_MODEL - D_CONV
GLA_HEADS = 4
D_GLA_K = D_GLA_V // 2
HEAD_K = D_GLA_K // GLA_HEADS
HEAD_V = D_GLA_V // GLA_HEADS
GATE_RANK = 16
GATE_NORMALIZER = 16.0
CHUNK = 64
CONV_WIDTH = 31
D_MIX = D_CONV + D_GLA_V
D_IN = 2 * D_CONV + 2 * D_GLA_K + 2 * D_GLA_V + GATE_RANK
N_GROUPS = 4
EXPERTS_PER_GROUP = 8
N_EXPERTS = N_GROUPS * EXPERTS_PER_GROUP
TOP_K = 2
D_EXPERT = D_MODEL // 2
MOE_BLOCK = 256
EPS = 1e-6

kernel_name = "hymba_conformer_gla_hmoe"

def rmsnorm(x, g):
    xf = x.astype(jnp.float32)
    y = xf * lax.rsqrt(jnp.mean(xf * xf, axis=-1, keepdims=True) + EPS)
    return (y * g.astype(jnp.float32)).astype(x.dtype)

def conformer_conv(u_a, u_gate, conv_w, conv_b, ln_g, ln_b):
    u = u_a * jax.nn.sigmoid(u_gate)
    y = lax.conv_general_dilated(
        u, conv_w[:, None, :].astype(u.dtype), window_strides=(1,),
        padding=((CONV_WIDTH - 1, 0),), dimension_numbers=('NWC', 'WIO', 'NWC'),
        feature_group_count=D_CONV) + conv_b
    yf = y.astype(jnp.float32)
    mu = jnp.mean(yf, axis=-1, keepdims=True)
    var = jnp.mean(jnp.square(yf - mu), axis=-1, keepdims=True)
    yf = (yf - mu) * lax.rsqrt(var + EPS) * ln_g.astype(jnp.float32) + ln_b.astype(jnp.float32)
    return jax.nn.silu(yf).astype(u.dtype)

def gla(q, k, v, g_out, gk_low, gk_w, gk_b, head_norm_g):
    B, S = q.shape[0], q.shape[1]
    n = S // CHUNK
    gk = jax.nn.log_sigmoid((gk_low @ gk_w + gk_b).astype(jnp.float32)) / GATE_NORMALIZER

    def heads(t, d):
        return t.reshape(B, n, CHUNK, GLA_HEADS, d).transpose(1, 0, 3, 2, 4).astype(jnp.float32)

    qh = heads(q, HEAD_K) * (HEAD_K ** -0.5)
    kh = heads(k, HEAD_K)
    vh = heads(v, HEAD_V)
    b = jnp.cumsum(heads(gk, HEAD_K), axis=3)
    b_last = b[..., -1:, :]
    q_t = qh * jnp.exp(b)
    k_t = kh * jnp.exp(-b)
    k_s = kh * jnp.exp(b_last - b)
    causal = jnp.tril(jnp.ones((CHUNK, CHUNK), dtype=bool))
    scores = jnp.where(causal, jnp.einsum('nbhik,nbhjk->nbhij', q_t, k_t), 0.0)
    o_intra = jnp.einsum('nbhij,nbhjv->nbhiv', scores, vh)

    def step(state, xs):
        q_c, k_c, v_c, dec = xs
        o = jnp.einsum('bhik,bhkv->bhiv', q_c, state)
        state = state * dec[:, :, 0, :, None] + jnp.einsum('bhjk,bhjv->bhkv', k_c, v_c)
        return state, o

    s0 = jnp.zeros((B, GLA_HEADS, HEAD_K, HEAD_V), jnp.float32)
    _, o_inter = lax.scan(step, s0, (q_t, k_s, vh, jnp.exp(b_last)))
    o = o_intra + o_inter
    o = o * lax.rsqrt(jnp.mean(o * o, axis=-1, keepdims=True) + EPS) * head_norm_g.astype(jnp.float32)
    o = o.transpose(1, 0, 3, 2, 4).reshape(B, S, D_GLA_V).astype(g_out.dtype)
    return o * jax.nn.silu(g_out)

def hier_moe(h, rg_w, rg_b, re_w, re_b, w_gate, w_up, w_down):
    B, S, D = h.shape
    T = B * S
    ht = h.reshape(T, D)
    grp_prob = jax.nn.softmax((ht @ rg_w).astype(jnp.float32) + rg_b.astype(jnp.float32), axis=-1)
    grp_p, grp_idx = lax.top_k(grp_prob, 1)
    exp_logits = (ht @ re_w).astype(jnp.float32).reshape(T, N_GROUPS, EXPERTS_PER_GROUP) + re_b.astype(jnp.float32)
    sel = exp_logits[jnp.arange(T), grp_idx[:, 0]]
    w_k, e_k = lax.top_k(jax.nn.softmax(sel, axis=-1), TOP_K)
    gate = grp_p * (w_k / jnp.sum(w_k, axis=-1, keepdims=True))
    eid = (grp_idx * EXPERTS_PER_GROUP + e_k).reshape(-1)

    A = T * TOP_K
    tok = jnp.repeat(jnp.arange(T, dtype=jnp.int32), TOP_K)
    order = jnp.argsort(eid)
    e_sorted = eid[order]
    counts = jnp.bincount(eid, length=N_EXPERTS)
    padded = (counts + MOE_BLOCK - 1) // MOE_BLOCK * MOE_BLOCK
    start = jnp.cumsum(counts) - counts
    pend = jnp.cumsum(padded)
    pstart = pend - padded
    dest_sorted = pstart[e_sorted] + (jnp.arange(A) - start[e_sorted])
    dest = jnp.zeros((A,), jnp.int32).at[order].set(dest_sorted.astype(jnp.int32))
    n_blocks = (A + MOE_BLOCK - 1) // MOE_BLOCK + N_EXPERTS
    cap = n_blocks * MOE_BLOCK
    row_tok = jnp.zeros((cap,), jnp.int32).at[dest].set(tok)
    block_expert = jnp.minimum(
        jnp.searchsorted(pend, jnp.arange(n_blocks) * MOE_BLOCK, side='right'), N_EXPERTS - 1)
    xb = ht[row_tok].reshape(n_blocks, MOE_BLOCK, D)

    def expert_block(args):
        xblk, e = args
        return (jax.nn.silu(xblk @ w_gate[e]) * (xblk @ w_up[e])) @ w_down[e]

    yb = lax.map(expert_block, (xb, block_expert)).reshape(cap, D)
    y = jnp.sum(yb[dest].reshape(T, TOP_K, D) * gate[..., None].astype(h.dtype), axis=1)
    return y.reshape(B, S, D)

def setup_inputs(seed: int = 0) -> dict:
    key = jax.random.key(seed)
    ks = jax.random.split(key, 24)
    f32 = jnp.float32
    nrm = lambda k, shape, s: jax.random.normal(k, shape, f32) * s
    L = DEPTH
    return {
        "x": nrm(ks[0], (BATCH, SEQ, D_MODEL), 1.0),
        "attn_norm_g": 1.0 + nrm(ks[1], (L, D_MODEL), 0.02),
        "w_in": nrm(ks[2], (L, D_MODEL, D_IN), D_MODEL ** -0.5),
        "conv_w": nrm(ks[3], (L, CONV_WIDTH, D_CONV), CONV_WIDTH ** -0.5),
        "conv_b": nrm(ks[4], (L, D_CONV), 0.01),
        "conv_ln_g": 1.0 + nrm(ks[5], (L, D_CONV), 0.02),
        "conv_ln_b": nrm(ks[6], (L, D_CONV), 0.01),
        "gk_w": nrm(ks[7], (L, GATE_RANK, D_GLA_K), GATE_RANK ** -0.5),
        "gk_b": nrm(ks[8], (L, D_GLA_K), 0.01),
        "gla_norm_g": 1.0 + nrm(ks[9], (L, HEAD_V), 0.02),
        "w_out": nrm(ks[10], (L, D_MIX, D_MODEL), D_MIX ** -0.5),
        "ffn_norm_g": 1.0 + nrm(ks[11], (L, D_MODEL), 0.02),
        "router_group_w": nrm(ks[12], (L, D_MODEL, N_GROUPS), D_MODEL ** -0.5),
        "router_group_b": nrm(ks[13], (L, N_GROUPS), 0.01),
        "router_expert_w": nrm(ks[14], (L, D_MODEL, N_EXPERTS), D_MODEL ** -0.5),
        "router_expert_b": nrm(ks[15], (L, N_GROUPS, EXPERTS_PER_GROUP), 0.01),
        "expert_w_gate": nrm(ks[16], (L, N_EXPERTS, D_MODEL, D_EXPERT), D_MODEL ** -0.5),
        "expert_w_up": nrm(ks[17], (L, N_EXPERTS, D_MODEL, D_EXPERT), D_MODEL ** -0.5),
        "expert_w_down": nrm(ks[18], (L, N_EXPERTS, D_EXPERT, D_MODEL), D_EXPERT ** -0.5),
        "final_norm_g": 1.0 + nrm(ks[19], (D_MODEL,), 0.02),
    }

def reference(x, attn_norm_g, w_in, conv_w, conv_b, conv_ln_g, conv_ln_b, gk_w, gk_b, gla_norm_g,
              w_out, ffn_norm_g, router_group_w, router_group_b, router_expert_w, router_expert_b,
              expert_w_gate, expert_w_up, expert_w_down, final_norm_g):
    splits = [D_CONV, 2 * D_CONV, 2 * D_CONV + D_GLA_K, 2 * D_CONV + 2 * D_GLA_K,
              2 * D_CONV + 2 * D_GLA_K + D_GLA_V, 2 * D_CONV + 2 * D_GLA_K + 2 * D_GLA_V]
    for l in range(DEPTH):
        hn = rmsnorm(x, attn_norm_g[l])
        proj = hn @ w_in[l]
        u_a, u_gate, q, k, v, g_out, gk_low = jnp.split(proj, splits, axis=-1)
        conv_out = conformer_conv(u_a, u_gate, conv_w[l], conv_b[l], conv_ln_g[l], conv_ln_b[l])
        gla_out = gla(q, k, v, g_out, gk_low, gk_w[l], gk_b[l], gla_norm_g[l])
        x = x + jnp.concatenate([conv_out, gla_out], axis=-1) @ w_out[l]
        hf = rmsnorm(x, ffn_norm_g[l])
        x = x + hier_moe(hf, router_group_w[l], router_group_b[l], router_expert_w[l], router_expert_b[l],
                         expert_w_gate[l], expert_w_up[l], expert_w_down[l])
    return rmsnorm(x, final_norm_g)


_drawn_inputs = setup_inputs


def setup_inputs(seed=0):
    import zlib

    import numpy as np

    out = dict(_drawn_inputs(seed))
    spreads = {}
    factors = {'conv_b': 4.146,
     'conv_ln_g': 8.99,
     'conv_ln_b': 17.89,
     'gk_b': 16.877,
     'gla_norm_g': 10.007,
     'router_group_b': 22.353,
     'router_expert_b': 19.89,
     'final_norm_g': 8.046,
     'ffn_norm_g': 3.835}
    for name, (base, spread) in spreads.items():
        noise = np.random.default_rng([zlib.crc32(name.encode()), seed]).standard_normal(out[name].shape)
        drawn = base * np.exp(spread * noise) if base else spread * noise
        out[name] = __import__('jax').numpy.asarray(drawn.astype(out[name].dtype))
    for name, factor in factors.items():
        out[name] = (out[name] * factor).astype(out[name].dtype)
    return out
```

```python
from contextlib import ExitStack

import concourse.bass as bass
from concourse import mybir

F32 = mybir.dt.float32
F32R = mybir.dt.float32r
I32 = mybir.dt.int32
U32 = mybir.dt.uint32
ALU = mybir.AluOpType
ACT = mybir.ActivationFunctionType
AX_X = mybir.AxisListType.X

P = 128
EPS = 1e-6


def layer_program(nc, x, attn_norm_g, w_in, conv_w, conv_b, conv_ln_g, conv_ln_b, gk_w, gk_b, gla_norm_g,
                  w_out, ffn_norm_g, router_group_w, router_group_b, router_expert_w, router_expert_b,
                  expert_w_gate, expert_w_up, expert_w_down, final_norm_g, out, CAP=128):
    _, T, D = x.shape
    NT = T // P
    KC = D // P
    TAPS, DC = conv_w.shape[1:]
    CT = DC // P
    RANK, DK = gk_w.shape[1:]
    HV = gla_norm_g.shape[1]
    HEADS = (D - DC) // HV
    HK = DK // HEADS
    PAIRS = DK // P
    CH = 64
    NCH = T // CH
    G = router_group_w.shape[2]
    NE = router_expert_w.shape[2]
    EG = NE // G
    NR = G + NE
    F = expert_w_gate.shape[3]
    FC = F // P
    HALF = T // 512
    A = 2 * T
    OV = A // CAP - 1
    NC = T // CAP
    OV_MAX = (OV + 1) // 2 * 2
    TILES = NE + OV_MAX + 1
    assert (D, DC, DK, HV, F, HK, PAIRS) == (1024, 512, 256, 128, 512, 64, 2)

    U_A, U_G, Q0, K0, V0, G0 = 0, DC, 2 * DC, 2 * DC + DK, 2 * DC + 2 * DK, 2 * DC + 2 * DK + HEADS * HV
    LOW0 = G0 + HEADS * HV
    W_COLS = [U_G, U_A, U_G + 256, U_A + 256, Q0, K0, V0, V0 + 256, G0, G0 + 256]
    N_IN = len(W_COLS)
    N_FRONT = N_IN + D // 256
    RW = 6
    RS = 4
    XS = 4
    PIECE = 2048

    x_v = x[0].rearrange("(t p) d -> t p d", p=P)
    out_v = out[0].rearrange("(t p) d -> t p d", p=P)
    w_in_v = w_in[0].rearrange("(j p) n -> p j n", p=P)
    w_out_v = w_out[0].rearrange("(j p) n -> p j n", p=P)
    wg_v = expert_w_gate[0].rearrange("e (p j) f -> e p j f", p=P)
    wu_v = expert_w_up[0].rearrange("e (p j) f -> e p j f", p=P)
    wd_v = expert_w_down[0].rearrange("e (p j) f -> e p j f", p=P)
    hf_dram = nc.dram_tensor("hf_rows", [T, D], F32).ap()
    y_dram = nc.dram_tensor("expert_rows", [A, D], F32).ap()
    hf_v = hf_dram.rearrange("(t p) d -> t p d", p=P)
    y_v = y_dram.rearrange("(k t p) d -> k t p d", p=P, k=2)

    with ExitStack() as ctx:
        here = [nc.sbuf_base + 31 & ~31]

        def at(name, shape, dt=F32, over=None):
            n = 4
            for s in shape[1:]:
                n *= s
            offset = here[0] if over is None else over
            if over is None:
                here[0] += n + 31 & ~31
            return nc.alloc_sbuf_tensor_at(name, shape, dt, offset=offset)

        raw = at("raw", [P, RW, PIECE])
        o_x2 = here[0]
        xnT = at("xnT", [P, KC, T])
        x2 = at("x2", [P, NT, D], over=o_x2)
        ident = at("ident", [P, P])
        upper = at("upper", [P, P])
        ones = at("ones", [P, P])
        ones_dc = at("ones_dc", [P, P])
        g_ffn = at("g_ffn", [P, D])
        g_fin = at("g_fin", [P, D])
        g_head = at("g_head", [P, HV])
        r_bias = at("r_bias", [P, NR])
        r_w = at("r_w", [P, KC, NR])
        prow = at("prow", [22, P])
        o_cw = here[0]
        cwrow = at("cwrow", [TAPS, DC])
        pcol = at("pcol", [P, 22 + CT * TAPS])
        gkw = at("gkw", [RANK, DK])
        w_low = at("w_low", [P, KC, RANK])
        stat = at("stat", [P, 8 * NT])
        hst = at("hst", [P, 3, HEADS * NT])
        cst = at("cst", [P, HEADS + 2])
        idx_g = at("idx_g", [P, TILES], I32)
        idx_s = at("idx_s", [P, TILES], I32)
        now_g = at("now_g", [P, 2], I32)
        now_s = at("now_s", [P, 2], I32)
        ov_info = at("ov_info", [P, OV_MAX + 1], I32)
        gates = at("gates", [P, 2, NT])
        dec = at("dec", [P, PAIRS, NCH])

        o_u = here[0]
        uT = at("uT", [P, CT, TAPS - 1 + T])
        acc = at("acc", [P, CT, T])
        o_q = here[0]
        qz = at("qz", [P, HEADS, T])
        o_kT = here[0]
        kT = at("kT", [P, PAIRS, T])
        o_sig = here[0]
        sig = at("sig", [P, 2, T])
        o_gla = here[0]
        glaT = at("glaT", [P, HEADS, T])
        xin = at("xin", [P, 2, D])
        o_ssb = here[0]
        ssb = at("ssb", [P, 2, HEADS * P])
        cmask = at("cmask", [P, HEADS * P])
        ksT = at("ksT", [P, PAIRS, P])
        kz = at("kz", [P, 2, PAIRS * P])
        o_st = here[0]
        st = at("st", [P, 4, PAIRS, 2 * HV])
        o_junk = here[0]
        junk = at("junk", [P, D])
        assert here[0] <= nc.sbuf_usable_end, (here[0], nc.sbuf_usable_end)
        hsq = at("hsq", [P, HEADS, HV], over=o_cw)
        sdv = at("sdv", [P, T], over=o_kT)
        xa = at("xa", [P, XS, D], over=o_gla)
        tmp1 = at("tmp1", [P, PAIRS, T], over=o_gla)
        tmp2 = at("tmp2", [P, PAIRS, T], over=o_gla + 4 * PAIRS * T)
        scanmask = at("scanmask", [P, T], over=o_ssb)
        lowT = at("lowT", [RANK, T], over=o_junk)
        gl = at("gl", [P, HEADS * HV], over=o_junk)
        vt = at("vt", [P, 2, HEADS * HV], over=o_sig)
        gg = at("gg", [P, 2, HEADS * HV], over=o_sig + 8 * HEADS * HV)
        sq = at("sq", [P, CT, T], over=o_u)
        hfp = at("hfp", [P, 2, D], over=o_u)
        hfT = at("hfT", [P, KC, P], over=o_u + 8 * D)
        logT = at("logT", [NR, T], over=o_u + 12 * D)
        here[0] = o_st
        iotaE = at("iotaE", [P, NE])
        iotaT = at("iotaT", [P, TILES])
        iotaR = at("iotaR", [P, CAP])
        iotaO = at("iotaO", [P, OV_MAX])
        desc = at("desc", [P, EG])
        tokid = at("tokid", [P, 2, 2, NT])
        here[0] = o_gla
        logit = at("logit", [P, NT, NR])
        msum = at("msum", [P, NT, NE])
        m_k = [at("m_k0", [P, NT, NE]), at("m_k1", [P, NT, NE])]
        rank = at("rank", [P, NT, NE])
        tots = at("tots", [P, NT + 1, NE])
        rt_a = at("rt_a", [P, NT, NE])
        small = at("small", [P, 48, NT])
        oneR = at("oneR", [P, 2, CAP])
        jcol = at("jcol", [P, 2, 2, TILES])
        evec = at("evec", [P, 8, NE])
        ovm = at("ovm", [P, OV_MAX, NE])
        ovn = at("ovn", [P, OV_MAX])
        w_hi = at("w_hi", [P, RS, PIECE], F32R, over=o_u)
        w_lo = at("w_lo", [P, RS, PIECE], F32R, over=o_q)
        here[0] = o_gla
        xg = at("xg", [P, D])
        xm_hi = at("xm_hi", [P, KC, P], F32R)
        xm_lo = at("xm_lo", [P, KC, P], F32R)
        ym = at("ym", [P, D])
        sg = at("sg", [P, F])
        hm = at("hm", [P, F])
        hm_hi = at("hm_hi", [P, FC, P], F32R)
        hm_lo = at("hm_lo", [P, FC, P], F32R)
        assert here[0] <= o_ssb
        yk = at("yk", [P, 2, 2, D], over=o_u)
        fin = at("fin", [P, 2, D], over=o_q)

        ps = ctx.enter_context(nc.psum_tensor("ps", [P, 8, 512], F32))

        def wide(n):
            return ps[:, n:n + 2, :].rearrange("p b n -> p (b n)")

        def sem(name):
            return ctx.enter_context(nc.semaphore(name))

        rows_in, low_in, late_in = sem("rows_in"), sem("low_in"), sem("late_in")
        xa_in = [sem(f"xa_in{i}") for i in range(XS)]
        x_in = [sem("x_in0"), sem("x_in1")]
        raw_in = [sem(f"raw_in{i}") for i in range(RW)]
        const_rdy = sem("const_rdy")
        zero_rdy = sem("zero_rdy")
        table_rdy = sem("table_rdy")
        pcol_ps, pcol_rdy = sem("pcol_ps"), sem("pcol_rdy")
        ss_rdy, rs_rdy = sem("ss_rdy"), sem("rs_rdy")
        pool_step = sem("pool_step")
        xs_rdy, tr_ps, xn_rdy = sem("xs_rdy"), sem("tr_ps"), sem("xn_rdy")
        w_used = sem("w_used")
        tg_ps, tg_act, tg_dve = sem("tg_ps"), sem("tg_act"), sem("tg_dve")
        abs_rdy, act_step, l_rdy = sem("abs_rdy"), sem("act_step"), sem("l_rdy")
        scan_rdy, e_rdy, dec_rdy = sem("scan_rdy"), sem("e_rdy"), sem("dec_rdy")
        conv_step, dve_step = sem("conv_step"), sem("dve_step")
        v_ps, g_ps, v_rdy, g_rdy, gg_rdy = sem("v_ps"), sem("g_ps"), sem("v_rdy"), sem("g_rdy"), sem("gg_rdy")
        ks_rdy, kt_ps, kz_rdy, kv_ps, st_rdy = sem("ks_rdy"), sem("kt_ps"), sem("kz_rdy"), sem("kv_ps"), sem("st_rdy")
        s_ps, ssb_rdy, o_ps = sem("s_ps"), sem("ssb_rdy"), sem("o_ps")
        hs_rdy, hr_rdy, gl_rdy, gt_ps, gla_rdy = sem("hs_rdy"), sem("hr_rdy"), sem("gl_rdy"), sem("gt_ps"), sem("gla_rdy")
        mu_ps, d_rdy, sq_rdy, var_ps = sem("mu_ps"), sem("d_rdy"), sem("sq_rdy"), sem("var_ps")
        sd_rdy, n_rdy, c_rdy = sem("sd_rdy"), sem("n_rdy"), sem("c_rdy")
        yo_ps, x2_rdy, hf_rdy = sem("yo_ps"), sem("x2_rdy"), sem("hf_rdy")
        hf_out = [sem("hf_out0"), sem("hf_out1")]
        th_ps, hfT_rdy, lg_ps, lgT_rdy, lt_ps = sem("th_ps"), sem("hfT_rdy"), sem("lg_ps"), sem("lgT_rdy"), sem("lt_ps")
        rt_in, rt_exp = sem("rt_in"), sem("rt_exp")
        ms_rdy, rank_ps = sem("ms_rdy"), sem("rank_ps")
        oh_rdy, oh_used, idx_rdy = sem("oh_rdy"), sem("oh_used"), sem("idx_rdy")
        g_in, xgt_ps = sem("g_in"), sem("xgt_ps")
        xh_rdy, xl_rdy = sem("xh_rdy"), sem("xl_rdy")
        hi_rdy, lo_rdy, split_used = sem("hi_rdy"), sem("lo_rdy"), sem("split_used")
        sg_rdy, hm_rdy, ht_ps = sem("sg_rdy"), sem("hm_rdy"), sem("ht_ps")
        hh_rdy, hl_rdy = sem("hh_rdy"), sem("hl_rdy")
        ya_rdy, yd_rdy, y_out = sem("ya_rdy"), sem("yd_rdy"), sem("y_out")
        ng_rdy, ns_rdy = sem("ng_rdy"), sem("ns_rdy")
        yk_in = [sem("yk_in0"), sem("yk_in1")]
        y0_rdy, x3_rdy, s3_rdy, r3_rdy, fin_rdy = sem("y0_rdy"), sem("x3_rdy"), sem("s3_rdy"), sem("r3_rdy"), sem("fin_rdy")
        out_done = [sem("out_done0"), sem("out_done1")]

        groups = [("low", 0, h) for h in range(HALF)]
        groups += [("gate", c, h) for c in (0, 1) for h in range(HALF)]
        groups += [("gk", c, h) for c in range(PAIRS) for h in range(HALF)]
        groups += [("a", c, h) for c in (0, 1) for h in range(HALF)]
        groups += [("gate", c, h) for c in (2, 3) for h in range(HALF)]
        groups += [("a", c, h) for c in (2, 3) for h in range(HALF)]
        groups += [("q", c, h) for c in range(PAIRS) for h in range(HALF)]
        groups += [("k", c, h) for c in range(PAIRS) for h in range(HALF)]
        by_act = {"low", "gate"}
        N_ACT = sum(g[0] in by_act for g in groups)
        N_DVE = len(groups) - N_ACT

        def evacuated(n):
            act = groups[n][0] in by_act
            same = [g for g in groups[:n + 1] if (g[0] in by_act) == act]
            return (tg_act if act else tg_dve), len(same)

        piece_of = {("gate", 0): 0, ("a", 0): 1, ("gate", 1): 2, ("a", 1): 3, ("q", 0): 4, ("k", 0): 5}
        front_uses = [sum(n % RW == s for n in range(N_FRONT)) for s in range(RW)]
        col_b, col_lg, col_lb, col_gk, col_w = 8, 12, 16, 20, 22

        def expert_pieces(e):
            return [wg_v[e, :, 0:4, :], wg_v[e, :, 4:8, :], wu_v[e, :, 0:4, :], wu_v[e, :, 4:8, :],
                    wd_v[e, :, 0:2, :], wd_v[e, :, 2:4, :]]

        def work_off_tiles(eng, start, tile):
            start(0, 0)
            tile(0, 0, True)
            tile(1, 1, True)
            with eng.Fori(1, NE // 2 - 1) as m:
                tile(2 * m, 0, True)
                tile(2 * m + 1, 1, True)
            tile(NE - 2, 0, True)
            tile(NE - 1, 1, False)
            n_over = eng.value_load(ov_info[0:1, OV_MAX:OV_MAX + 1], min_val=0, max_val=OV)
            with eng.If(n_over > 0):
                with eng.Fori(NE // 2, NE // 2 + OV_MAX // 2) as m:
                    for b in range(2):
                        with eng.If(n_over > 2 * m + (b - NE)):
                            start(2 * m + b, b)
                            tile(2 * m + b, b, False)

        block = ctx.enter_context(nc.Block())

        @block.sync
        def _(sp):
            def load_xa(i):
                if i >= XS:
                    sp.wait_ge(tr_ps, i - XS + 1)
                sp.dma_start(xa[:, i % XS, :], x_v[i]).then_inc(xa_in[i % XS], 16)

            def load_x(i):
                if i >= 2:
                    sp.wait_ge(x2_rdy, i - 1)
                sp.dma_start(xin[:, i % 2, :], x_v[i]).then_inc(x_in[i % 2], 16)

            def load_front(n):
                if n >= RW:
                    sp.wait_ge(w_used, n - RW + 1)
                v = w_in_v[:, :, W_COLS[n]:W_COLS[n] + 256] if n < N_IN \
                    else w_out_v[:, :, (n - N_IN) * 256:(n - N_IN + 1) * 256]
                sp.dma_start(raw[:, n % RW, :].rearrange("p (j n) -> p j n", n=256), v).then_inc(raw_in[n % RW], 16)

            for i in range(XS):
                load_xa(i)
                if i == 1:
                    load_front(0)
            for i in range(XS, NT):
                load_xa(i)
                load_front(i - XS + 1)
            load_front(RW - 1)
            for n in range(RW, N_FRONT):
                load_front(n)
                if n == N_IN - 1:
                    load_x(0)
                    load_x(1)
            order = sorted(range(RW), key=lambda s: (front_uses[s] - 1) * RW + s)
            for i, s in enumerate(order):
                sp.wait_ge(w_used, (front_uses[s] - 1) * RW + s + 1)
                sp.dma_start(raw[:, s, :].rearrange("p (j n) -> p j n", n=D if s >= 4 else F),
                             expert_pieces(0)[s]).then_inc(raw_in[s], 16)
                if i == 1:
                    for t in range(2, NT):
                        load_x(t)

            def load_expert(e, w):
                for i, v in enumerate(expert_pieces(w)):
                    sp.wait_ge(lo_rdy, 6 * e - 5 + i)
                    sp.dma_start(raw[:, i, :].rearrange("p (j n) -> p j n", n=D if i >= 4 else F), v)\
                        .then_inc(raw_in[i], 16)

            with sp.Fori(1, NE) as e:
                load_expert(e, e)
            sp.wait_ge(idx_rdy, 2)

            n_over = sp.value_load(ov_info[0:1, OV_MAX:OV_MAX + 1], min_val=0, max_val=OV)
            with sp.If(n_over > 0):
                with sp.Fori(0, OV_MAX) as j:
                    with sp.If(n_over > j):
                        e = sp.value_load(ov_info[0:1, bass.ds(j, 1)], min_val=0, max_val=NE - 1)
                        load_expert(j + NE, e)
            sp.wait_ge(y_out, (n_over + NE) * 16)
            for t in range(NT):
                for k in range(2):
                    if t >= 2:
                        sp.wait_ge(x3_rdy, t - 1)
                    sp.dma_start(yk[:, t % 2, k, :], y_v[k, t]).then_inc(yk_in[t % 2], 16)
            for s in range(2):
                sp.wait_ge(out_done[s], 16 * (NT // 2))
            for s in range(2):
                sp.wait_ge(hf_out[s], 16 * (NT // 2))

        @block.gpsimd
        def _(pool):
            n_const = [0]

            def const(ins):
                n_const[0] += 1
                ins.then_inc(const_rdy, 1)

            def settle():
                pool.wait_ge(const_rdy, n_const[0])

            const(pool.memset(ident[:], 0.0))
            settle()
            const(pool.affine_select(out=ident[:], in_=ident[:], compare_op=ALU.not_equal, fill=1.0, base=0,
                                     pattern=[[-1, P]], channel_multiplier=1))
            pool.memset(cst[:, 0:HEADS], -0.5)
            pool.memset(cst[:, HEADS:HEADS + 1], EPS)
            pool.memset(cst[:, HEADS + 1:HEADS + 2], 1.0)
            const(pool.memset(uT[:, :, 0:TAPS - 1], 0.0))
            settle()

            def rms(n, src, mid, dst, width, scale, done):
                pool.tensor_scalar(mid, src, scale, EPS, ALU.mult, ALU.add).then_inc(pool_step, 1)
                steps[0] += 1
                pool.wait_ge(pool_step, steps[0])
                pool.tensor_tensor(dst, mid, cst[:, 0:width], ALU.pow).then_inc(done, 1)

            steps = [0]
            for i in range(NT):
                pool.wait_ge(ss_rdy, i + 1)
                rms(i, stat[:, i:i + 1], stat[:, 8 + i:9 + i], stat[:, 16 + i:17 + i], 1, 1.0 / D, rs_rdy)
                if i == 0:
                    const(pool.memset(scanmask[:], 1.0))
                    settle()
                    const(pool.memset(scanmask[:, 0:T:CH], 0.0))
                    const(pool.memset(qz[:], 0.0))
            for dst, src in ((g_ffn[:], ffn_norm_g[0:1, :].broadcast_to([P, D])),
                             (g_fin[:], final_norm_g.unsqueeze(0).broadcast_to([P, D])),
                             (g_head[:], gla_norm_g[0:1, :].broadcast_to([P, HV])),
                             (r_bias[:, 0:G], router_group_b[0:1, :].broadcast_to([P, G])),
                             (r_bias[:, G:NR], router_expert_b.rearrange("l g e -> l (g e)").broadcast_to([P, NE])),
                             (r_w[:, :, 0:G], router_group_w[0].rearrange("(p j) n -> p j n", j=KC)),
                             (r_w[:, :, G:NR], router_expert_w[0].rearrange("(p j) n -> p j n", j=KC))):
                pool.dma_start(dst, src).then_inc(late_in, 16)
            const(pool.memset(ones[:], 1.0))
            pool.memset(ones_dc[:], 1.0 / DC)
            pool.memset(kz[:], 0.0)
            pool.memset(st[:, 0, :, :], 0.0)
            const(pool.memset(cmask[:], 1.0))
            settle()
            const(pool.affine_select(out=upper[:], in_=ones[:], compare_op=ALU.is_gt, fill=0.0, base=0,
                                     pattern=[[1, P]], channel_multiplier=-1))
            const(pool.affine_select(out=cmask[:].rearrange("p (h i) -> p h i", h=HEADS),
                                     in_=cmask[:].rearrange("p (h i) -> p h i", h=HEADS), compare_op=ALU.is_ge,
                                     fill=0.0, base=0, pattern=[[0, HEADS], [1, P]], channel_multiplier=-1))
            settle()
            const(pool.memset(cmask[0:CH, :].rearrange("p (h i) -> p h i", h=HEADS)[:, :, CH:P], 0.0))
            pool.wait_ge(e_rdy, 1)
            pool.tensor_copy(dec[:], tmp2[:, :, CH - 1:T:CH]).then_inc(dec_rdy, 1)
            pool.wait_ge(scan_rdy, PAIRS)
            pool.memset(ssb[:], 0.0).then_inc(zero_rdy, 1)
            for t in range(NT):
                pool.wait_ge(late_in, 16 * 7)
                pool.wait_ge(g_rdy, t + 1)
                v = gg[:, t % 2, :].rearrange("p (h v) -> p h v", h=HEADS)
                pool.tensor_tensor(v, v, g_head[:].unsqueeze(1).broadcast_to([P, HEADS, HV]), ALU.mult)\
                    .then_inc(gg_rdy, 1)
                pool.wait_ge(hs_rdy, t + 1)
                c = slice(t * HEADS, (t + 1) * HEADS)
                rms(t, hst[:, 0, c], hst[:, 1, c], hst[:, 2, c], HEADS, 1.0 / HV, hr_rdy)
            pool.wait_ge(o_ps, NT)
            pool.wait_ge(st_rdy, 2 * NT)
            pool.iota(iotaE[:], pattern=[[1, NE]], base=0, channel_multiplier=0, allow_small_or_imprecise_dtypes=True)
            pool.iota(iotaT[:], pattern=[[1, TILES]], base=0, channel_multiplier=0, allow_small_or_imprecise_dtypes=True)
            pool.iota(iotaR[:], pattern=[[1, CAP]], base=0, channel_multiplier=0, allow_small_or_imprecise_dtypes=True)
            pool.iota(iotaO[:], pattern=[[1, OV_MAX]], base=0, channel_multiplier=0, allow_small_or_imprecise_dtypes=True)
            pool.iota(desc[:], pattern=[[-1, EG]], base=EG, channel_multiplier=0, allow_small_or_imprecise_dtypes=True)
            for k in range(2):
                pool.iota(tokid[:, 0, k, :], pattern=[[P, NT]], base=-A, channel_multiplier=1, allow_small_or_imprecise_dtypes=True)
                last = pool.iota(tokid[:, 1, k, :], pattern=[[P, NT]], base=k * T - 2 * A, channel_multiplier=1, allow_small_or_imprecise_dtypes=True)
            last.then_inc(table_rdy, 1)
            for t in range(NT):
                pool.wait_ge(ss_rdy, NT + t + 1)
                rms(t, stat[:, 24 + t:25 + t], stat[:, 32 + t:33 + t], stat[:, 40 + t:41 + t], 1, 1.0 / D, rs_rdy)

            pool.wait_ge(idx_rdy, 3)
            for s in range(2):
                pool.wait_ge(hf_out[s], 16 * (NT // 2))

            pool.tensor_copy(now_g[:, 0:1], idx_g[:, 0:1]).then_inc(ng_rdy, 1)
            pool.tensor_copy(now_s[:, 0:1], idx_s[:, 0:1]).then_inc(ns_rdy, 1)

            def gather(e, b):
                if not (isinstance(e, int) and e == 0):
                    pool.wait_ge(xgt_ps, e)
                    pool.wait_ge(g_in, 16 * e)
                pool.wait_ge(ng_rdy, e + 1)
                pool.tensor_copy(now_g[:, 1 - b:2 - b], idx_g[:, bass.ds(e + 1, 1)]).then_inc(ng_rdy, 1)
                pool.indirect_dma_start(
                    out=xg[:], out_offset=None, in_=hf_dram,
                    in_offset=bass.IndirectOffsetOnAxis(ap=now_g[:, b:b + 1].bitcast(U32), axis=0),
                    bounds_check=T - 1, oob_is_err=False).then_inc(g_in, 16)

            def start(e, b):
                gather(e, b)
                if isinstance(e, int):
                    gather(e + 1, 1 - b)

            def tile(e, b, more):
                if more and not (isinstance(e, int) and e == NE - 2):
                    gather(e + 2, b)
                if not (isinstance(e, int) and e == 0):
                    pool.wait_ge(y_out, 16 * e)
                pool.wait_ge(ns_rdy, e + 1)
                pool.wait_ge(ya_rdy, e + 1)
                pool.wait_ge(yd_rdy, e + 1)
                pool.tensor_copy(now_s[:, 1 - b:2 - b], idx_s[:, bass.ds(e + 1, 1)]).then_inc(ns_rdy, 1)
                pool.indirect_dma_start(
                    out=y_dram, out_offset=bass.IndirectOffsetOnAxis(ap=now_s[:, b:b + 1].bitcast(U32), axis=0),
                    in_=ym[:], in_offset=None, bounds_check=A - 1, oob_is_err=False).then_inc(y_out, 16)

            work_off_tiles(pool, start, tile)
            for t in range(NT):
                pool.wait_ge(s3_rdy, t + 1)
                pool.tensor_scalar(stat[:, 8 + t:9 + t], stat[:, 48 + t:49 + t], 1.0 / D, EPS, ALU.mult, ALU.add)\
                    .then_inc(pool_step, 1)
                steps[0] += 1
                pool.wait_ge(pool_step, steps[0])
                pool.tensor_tensor(stat[:, 56 + t:57 + t], stat[:, 8 + t:9 + t], cst[:, 0:1], ALU.pow)\
                    .then_inc(r3_rdy, 1)

        @block.scalar
        def _(act):
            for v, r in ((attn_norm_g[0], 0), (conv_b[0], col_b), (conv_ln_g[0], col_lg), (conv_ln_b[0], col_lb),
                         (gk_b[0], col_gk)):
                v = v.rearrange("(r p) -> r p", p=P)
                act.dma_start(prow[r:r + v.shape[0], :], v).then_inc(rows_in, 16)
            act.dma_start(cwrow[:], conv_w[0]).then_inc(rows_in, 16)
            act.dma_start(w_low[:], w_in_v[:, :, LOW0:LOW0 + RANK]).then_inc(low_in, 16)
            act.dma_start(gkw[:], gk_w[0]).then_inc(low_in, 16)
            for i in range(NT):
                act.wait_ge(xa_in[i % XS], 16 * (i // XS + 1))
                if i:
                    act.wait_ge(ss_rdy, i)
                act.activation(junk[:], xa[:, i % XS, :], ACT.Square, accum_out=stat[:, i:i + 1]).then_inc(ss_rdy, 1)
            act.wait_ge(ss_rdy, NT)
            act.wait_ge(const_rdy, 3)
            act.wait_ge(pcol_rdy, 1)
            steps = [0]

            def step(ins):
                steps[0] += 1
                ins.then_inc(act_step, 1)
                act.wait_ge(act_step, steps[0])

            n_abs = 0
            for n, (what, c, h) in enumerate(groups):
                cols = slice(h * 512, (h + 1) * 512)
                if what == "low":
                    act.wait_ge(tg_ps, n + 1)
                    act.activation(lowT[:, cols], ps[0:RANK, n % 4, :], ACT.Copy).then_inc(tg_act, 1)
                elif what == "gate":
                    act.wait_ge(tg_ps, n + 1)
                    if c >= 2:
                        act.wait_ge(*evacuated(groups.index(("a", c - 2, h))))
                    act.activation(sig[:, c % 2, cols], ps[:, n % 4, :], ACT.Sigmoid).then_inc(tg_act, 1)
                elif what == "gk":
                    act.wait_ge(tg_ps, n + 1)
                    act.activation(tmp1[:, c, cols], ps[:, n % 4, :], ACT.Abs, bias=pcol[:, col_gk + c:col_gk + c + 1])\
                        .then_inc(abs_rdy, 1)
                    n_abs += 1
                    if n_abs == PAIRS * HALF:
                        act.wait_ge(abs_rdy, n_abs)
                        step(act.activation(tmp1[:], tmp1[:], ACT.Exp, scale=-1.0))
                        act.activation(tmp1[:], tmp1[:], ACT.Ln, bias=cst[:, HEADS + 1:HEADS + 2]).then_inc(l_rdy, 1)
            act.wait_ge(scan_rdy, PAIRS)
            act.activation(tmp2[:], tmp1[:], ACT.Exp, scale=1.0 / 16).then_inc(e_rdy, 1)
            act.wait_ge(e_rdy, 1)
            act.activation(tmp1[:], tmp1[:], ACT.Exp, scale=-1.0 / 16).then_inc(e_rdy, 1)

            def scaled_keys(t):
                act.wait_ge(dec_rdy, 1)
                act.wait_ge(tg_dve, N_DVE)
                if t:
                    act.wait_ge(kt_ps, t)
                for pr in range(PAIRS):
                    for c in range(2):
                        tok = slice(t * P + c * CH, t * P + (c + 1) * CH)
                        last = act.activation(ksT[:, pr, c * CH:(c + 1) * CH], kT[:, pr, tok], ACT.Copy,
                                              scale=dec[:, pr, 2 * t + c:2 * t + c + 1])
                last.then_inc(ks_rdy, 1)

            def values(t):
                act.wait_ge(v_ps, t + 1)
                if t >= 2:
                    act.wait_ge(o_ps, t - 1)
                act.activation(vt[:, t % 2, :], ps[:, 0, :], ACT.Copy).then_inc(v_rdy, 1)

            def gate_out(t):
                act.wait_ge(g_ps, t + 1)
                if t >= 2:
                    act.wait_ge(gl_rdy, t - 1)
                act.activation(gg[:, t % 2, :], ps[:, 1, :], ACT.Silu).then_inc(g_rdy, 1)

            def gla_columns(t):
                act.wait_ge(gt_ps, t + 1)
                act.activation(glaT[:, :, t * P:(t + 1) * P], ps[:, 7, :].rearrange("p (h i) -> p h i", h=HEADS),
                               ACT.Copy).then_inc(gla_rdy, 1)

            scaled_keys(0)
            values(0)
            gate_out(0)
            for t in range(NT):
                act.wait_ge(kt_ps, t + 1)
                if t:
                    act.wait_ge(kv_ps, t)
                act.activation(kz[0:CH, 0, :], ps[0:CH, 6, 0:PAIRS * P], ACT.Copy)
                act.activation(kz[CH:P, 1, :], ps[CH:P, 6, 0:PAIRS * P], ACT.Copy).then_inc(kz_rdy, 1)
                if t + 1 < NT:
                    values(t + 1)
                if t:
                    gla_columns(t - 1)
                if t + 1 < NT:
                    gate_out(t + 1)
                    scaled_keys(t + 1)
                act.wait_ge(o_ps, t + 1)
                if t:
                    act.wait_ge(hs_rdy, t)
                for h in range(HEADS):
                    last = act.activation(hsq[:, h, :], ps[:, 2, h * HV:(h + 1) * HV], ACT.Square,
                                          accum_out=hst[:, 0, t * HEADS + h:t * HEADS + h + 1])
                last.then_inc(hs_rdy, 1)
            gla_columns(NT - 1)
            for h in range(HALF):
                act.wait_ge(d_rdy, h + 1)
                act.activation(sq[:, :, h * 512:(h + 1) * 512], acc[:, :, h * 512:(h + 1) * 512], ACT.Square)\
                    .then_inc(sq_rdy, 1)
            for h in range(HALF):
                act.wait_ge(var_ps, h + 1)
                act.activation(sdv[:, h * 512:(h + 1) * 512], ps[:, 2 + h, :], ACT.Sqrt, bias=cst[:, HEADS:HEADS + 1])\
                    .then_inc(sd_rdy, 1)
            for h in range(HALF):
                act.wait_ge(n_rdy, h + 1)
                for c in range(CT):
                    v = acc[:, c, h * 512:(h + 1) * 512]
                    act.activation(v, v, ACT.Silu, scale=pcol[:, col_lg + c:col_lg + c + 1],
                                   bias=pcol[:, col_lb + c:col_lb + c + 1]).then_inc(c_rdy, 1)
            for t in range(NT + 1):
                if t < NT:
                    act.wait_ge(x2_rdy, t + 1)
                    act.wait_ge(ss_rdy, NT + t)
                    act.activation(junk[:], x2[:, t, :], ACT.Square, accum_out=stat[:, 24 + t:25 + t])\
                        .then_inc(ss_rdy, 1)
                    act.wait_ge(hf_rdy, t + 1)
                    act.dma_start(hf_v[t], hfp[:, t % 2, :]).then_inc(hf_out[t % 2], 16)
                    act.wait_ge(th_ps, t + 1)
                    if t:
                        act.wait_ge(lg_ps, t)
                    act.activation(hfT[:].rearrange("p j i -> p (j i)"), wide(4), ACT.Copy).then_inc(hfT_rdy, 1)
                    act.wait_ge(lg_ps, t + 1)
                    act.activation(logT[:, t * P:(t + 1) * P], ps[0:NR, 6, 0:P], ACT.Copy).then_inc(lgT_rdy, 1)
            act.wait_ge(rt_in, 1)
            act.activation(rt_a[:, :, 8:8 + G], rt_a[:, :, 0:G], ACT.Exp).then_inc(rt_exp, 1)
            act.wait_ge(rt_in, 2)
            act.activation(small[:, 6, :], small[:, 5, :], ACT.Exp).then_inc(rt_exp, 1)

            def split_hi(e, i, b):
                k = 6 * e + i
                act.wait_ge(raw_in[i], 16 * (front_uses[i] + 1) + 16 * e)
                if not (isinstance(e, int) and k < RS):
                    act.wait_ge(split_used, k - RS + 1)
                act.activation(w_hi[:, (6 * b + i) % RS, :], raw[:, i, :], ACT.Copy).then_inc(hi_rdy, 1)

            def x_hi(e):
                act.wait_ge(xgt_ps, e + 1)
                if not (isinstance(e, int) and e == 0):
                    act.wait_ge(split_used, 6 * e - 2)
                act.activation(xm_hi[:].rearrange("p j i -> p (j i)"), wide(2), ACT.Copy).then_inc(xh_rdy, 1)

            act.wait_ge(lgT_rdy, NT)
            act.wait_ge(lt_ps, NT)
            for s in range(2):
                act.wait_ge(hf_out[s], 16 * (NT // 2))

            def start(e, b):
                for i in range(4):
                    split_hi(e, i, b)
                x_hi(e)

            def tile(e, b, more):
                split_hi(e, 4, b)
                split_hi(e, 5, b)
                act.wait_ge(split_used, 6 * e + 2)
                act.activation(sg[:], ps[:, 0, :], ACT.Silu).then_inc(sg_rdy, 1)
                if more:
                    split_hi(e + 1, 0, 1 - b)
                act.wait_ge(ht_ps, e + 1)
                act.activation(hm_hi[:].rearrange("p j i -> p (j i)"), ps[:, 4, :], ACT.Copy).then_inc(hh_rdy, 1)
                if more:
                    x_hi(e + 1)
                    split_hi(e + 1, 1, 1 - b)
                act.wait_ge(split_used, 6 * e + 6)
                if not (isinstance(e, int) and e == 0):
                    act.wait_ge(y_out, 16 * e)
                act.activation(ym[:, 0:512], ps[:, 5, :], ACT.Copy).then_inc(ya_rdy, 1)
                if more:
                    split_hi(e + 1, 2, 1 - b)
                    split_hi(e + 1, 3, 1 - b)

            work_off_tiles(act, start, tile)
            for t in range(NT):
                act.wait_ge(x3_rdy, t + 1)
                if t:
                    act.wait_ge(s3_rdy, t)
                act.activation(junk[:], x2[:, t, :], ACT.Square, accum_out=stat[:, 48 + t:49 + t]).then_inc(s3_rdy, 1)
                if t:
                    act.wait_ge(fin_rdy, t)
                    act.dma_start(out_v[t - 1], fin[:, (t - 1) % 2, :]).then_inc(out_done[(t - 1) % 2], 16)
            act.wait_ge(fin_rdy, NT)
            act.dma_start(out_v[NT - 1], fin[:, (NT - 1) % 2, :]).then_inc(out_done[(NT - 1) % 2], 16)

        @block.vector
        def _(dve):
            steps = [0]

            def step(ins):
                steps[0] += 1
                ins.then_inc(dve_step, 1)
                dve.wait_ge(dve_step, steps[0])

            dve.wait_ge(pcol_ps, 1)
            dve.tensor_copy(pcol[:], ps[:, 0, 0:22 + CT * TAPS]).then_inc(pcol_rdy, 1)
            dve.wait_ge(pcol_rdy, 1)
            g_col = pcol[:, 0:KC].unsqueeze(2).broadcast_to([P, KC, P])
            for i in range(NT + 1):
                if i < NT:
                    dve.wait_ge(rs_rdy, i + 1)
                    v = xa[:, i % XS, :]
                    dve.tensor_scalar(v, v, stat[:, 16 + i:17 + i], None, ALU.mult).then_inc(xs_rdy, 1)
                if i:
                    t = i - 1
                    dve.wait_ge(tr_ps, t + 1)
                    dve.tensor_tensor(xnT[:, :, t * P:(t + 1) * P],
                                      wide(4 + 2 * (t % 2)).rearrange("p (j i) -> p j i", j=KC), g_col, ALU.mult)\
                        .then_inc(xn_rdy, 1)

            def conv_ops():
                n = 0
                for c in range(CT):
                    for w in range(TAPS):
                        tap = pcol[:, col_w + c * TAPS + w:col_w + c * TAPS + w + 1]
                        src = uT[:, c, w:w + T]
                        if w == 0:
                            ins = dve.tensor_scalar(acc[:, c, :], src, tap, pcol[:, col_b + c:col_b + c + 1],
                                                    ALU.mult, ALU.add)
                        else:
                            dve.wait_ge(conv_step, n)
                            ins = dve.scalar_tensor_tensor(acc[:, c, :], src, tap, acc[:, c, :], ALU.mult, ALU.add)
                        n += 1
                        yield ins.then_inc(conv_step, 1)

            convolution = conv_ops()

            def conv(n):
                for _ in range(n):
                    next(convolution, None)

            dve.wait_ge(const_rdy, 3)
            n_gk = 0
            before = {("a", 2, 0): 22, ("a", 2, 1): 5, ("a", 3, 0): 5, ("a", 3, 1): 5}
            for n, (what, c, h) in enumerate(groups):
                cols = slice(h * 512, (h + 1) * 512)
                if what == "gk":
                    dve.wait_ge(abs_rdy, n_gk + 1)
                    n_gk += 1
                    dve.tensor_scalar(tmp2[:, c, cols], ps[:, n % 4, :], pcol[:, col_gk + c:col_gk + c + 1], 0.0,
                                      ALU.add, ALU.min).then_inc(tg_dve, 1)
                    if n_gk == PAIRS * HALF:
                        dve.wait_ge(tg_dve, n_gk)
                        dve.wait_ge(l_rdy, 1)
                        step(dve.tensor_tensor(tmp2[:], tmp2[:], tmp1[:], ALU.subtract))
                        dve.wait_ge(const_rdy, 5)
                        for pr in range(PAIRS):
                            dve.tensor_tensor_scan(tmp1[:, pr, :], scanmask[:], tmp2[:, pr, :], 0.0,
                                                   ALU.mult, ALU.add).then_inc(scan_rdy, 1)
                elif what == "a":
                    conv(before.get((what, c, h), 0))
                    dve.wait_ge(tg_ps, n + 1)
                    dve.wait_ge(*evacuated(groups.index(("gate", c, h))))
                    dve.tensor_tensor(uT[:, c, TAPS - 1 + h * 512:TAPS - 1 + (h + 1) * 512], ps[:, n % 4, :],
                                      sig[:, c % 2, cols], ALU.mult).then_inc(tg_dve, 1)
                    dve.wait_ge(*evacuated(n))
                elif what == "q":
                    conv(4)
                    dve.wait_ge(tg_ps, n + 1)
                    dve.wait_ge(e_rdy, 1)
                    dve.wait_ge(const_rdy, 6)
                    for r in range(2):
                        rows = slice(r * HK, (r + 1) * HK)
                        last = dve.scalar_tensor_tensor(qz[rows, 2 * c + r, cols], ps[rows, n % 4, :], HK ** -0.5,
                                                        tmp2[rows, c, cols], ALU.mult, ALU.mult)
                    last.then_inc(tg_dve, 1)
                elif what == "k":
                    conv(4)
                    dve.wait_ge(tg_ps, n + 1)
                    dve.wait_ge(e_rdy, 2)
                    dve.tensor_tensor(kT[:, c, cols], ps[:, n % 4, :], tmp1[:, c, cols], ALU.mult).then_inc(tg_dve, 1)

            dve.wait_ge(const_rdy, 11)
            dve.wait_ge(zero_rdy, 1)
            for t in range(NT):
                dve.wait_ge(s_ps, t + 1)
                if t >= 2:
                    dve.wait_ge(o_ps, t - 1)
                dve.copy_predicated(ssb[:, t % 2, :], cmask[:].bitcast(I32), ps[:, 3, :]).then_inc(ssb_rdy, 1)
                conv(3)
                dve.wait_ge(dec_rdy, 1)
                dve.wait_ge(kv_ps, t + 1)
                for c in range(2):
                    n = 2 * t + c
                    if n:
                        dve.wait_ge(st_rdy, n)
                    if n >= 3:
                        dve.wait_ge(o_ps, (n - 3) // 2 + 1)
                    for pr in range(PAIRS):
                        last = dve.scalar_tensor_tensor(
                            st[:, (n + 1) % 4, pr, :], st[:, n % 4, pr, :], dec[:, pr, n:n + 1],
                            ps[:, 4 + c, pr * 2 * HV:(pr + 1) * 2 * HV], ALU.mult, ALU.add)
                    last.then_inc(st_rdy, 1)
                conv(3)
                dve.wait_ge(hr_rdy, t + 1)
                dve.wait_ge(gg_rdy, t + 1)
                if t:
                    dve.wait_ge(gt_ps, t)
                for h in range(HEADS):
                    cols = slice(h * HV, (h + 1) * HV)
                    last = dve.scalar_tensor_tensor(gl[:, cols], ps[:, 2, cols],
                                                    hst[:, 2, t * HEADS + h:t * HEADS + h + 1],
                                                    gg[:, t % 2, cols], ALU.mult, ALU.mult)
                last.then_inc(gl_rdy, 1)
            conv(CT * TAPS)
            dve.wait_ge(conv_step, CT * TAPS)
            for h in range(HALF):
                v = acc[:, :, h * 512:(h + 1) * 512]
                dve.wait_ge(mu_ps, h + 1)
                dve.tensor_tensor(v, v, ps[:, h, :].unsqueeze(1).broadcast_to([P, CT, 512]), ALU.subtract)\
                    .then_inc(d_rdy, 1)
            dve.wait_ge(d_rdy, HALF)
            for h in range(HALF):
                v, r = acc[:, :, h * 512:(h + 1) * 512], sdv[:, h * 512:(h + 1) * 512]
                dve.wait_ge(sd_rdy, h + 1)
                step(dve.reciprocal(r, r))
                dve.wait_ge(sq_rdy, h + 1)
                dve.tensor_tensor(v, v, r.unsqueeze(1).broadcast_to([P, CT, 512]), ALU.mult).then_inc(n_rdy, 1)
            dve.wait_ge(late_in, 16 * 7)
            for t in range(NT):
                dve.wait_ge(yo_ps, t + 1)
                dve.wait_ge(x_in[t % 2], 16 * (t // 2 + 1))
                dve.tensor_tensor(x2[:, t, :], wide(2 * (t % 2)), xin[:, t % 2, :], ALU.add).then_inc(x2_rdy, 1)
                dve.wait_ge(rs_rdy, NT + t + 1)
                if t >= 2:
                    dve.wait_ge(hf_out[t % 2], 16 * (t // 2))
                    dve.wait_ge(th_ps, t - 1)
                dve.scalar_tensor_tensor(
                    hfp[:, t % 2, :].rearrange("p (j q) -> p j q", j=KC),
                    x2[:, t, :].rearrange("p (q j) -> p j q", j=KC), stat[:, 40 + t:41 + t],
                    g_ffn[:].rearrange("p (q j) -> p j q", j=KC), ALU.mult, ALU.mult).then_inc(hf_rdy, 1)

            dve.wait_ge(lt_ps, NT)
            dve.wait_ge(yo_ps, NT)
            dve.wait_ge(table_rdy, 1)
            s = [small[:, i, :] for i in range(22)]
            gmax, gsum, gp, m1, m2, dm, ed, one_ed, r_ed = s[0:9]
            rk, ek, obk, ck = s[9:11], s[11:13], s[13:15], s[15:17]
            tc, rr = s[17:19], s[19:21]

            def over(v, shape, axis):
                return v.unsqueeze(axis).broadcast_to([P] + shape)

            def first_max(hot, vals, top, scratch, n):
                shape = [NT, n]
                step(dve.tensor_tensor(hot, vals, over(top, shape, 2), ALU.is_equal))
                step(dve.tensor_tensor(hot, hot, over(desc[:, EG - n:EG], shape, 1), ALU.mult))
                step(dve.tensor_reduce(scratch, hot, AX_X, ALU.max))
                step(dve.tensor_tensor(hot, hot, over(scratch, shape, 2), ALU.is_equal))

            step(dve.tensor_tensor(logit[:], ps[:, 7, 0:NT * NR].rearrange("p (t n) -> p t n", n=NR),
                                   over(r_bias[:], [NT, NR], 1), ALU.add))
            lg, le = logit[:, :, 0:G], logit[:, :, G:NR].rearrange("p t (g e) -> p t g e", g=G)
            step(dve.tensor_reduce(gmax, lg, AX_X, ALU.max))
            dve.tensor_tensor(rt_a[:, :, 0:G], lg, over(gmax, [NT, G], 2), ALU.subtract).then_inc(rt_in, 1)
            hot_g = rt_a[:, :, 16:16 + G]
            first_max(hot_g, lg, gmax, s[21], G)
            sel4 = rank[:].rearrange("p t (g e) -> p t g e", g=G)
            for g in range(G):
                last = dve.tensor_tensor(sel4[:, :, g, :], le[:, :, g, :],
                                         hot_g[:, :, g:g + 1].broadcast_to([P, NT, EG]), ALU.mult)
            step(last)
            sel, sel2 = msum[:, :, 0:EG], msum[:, :, EG:2 * EG]
            hot = [msum[:, :, 2 * EG:3 * EG], msum[:, :, 3 * EG:4 * EG]]
            step(dve.tensor_reduce(sel, sel4.rearrange("p t g e -> p t e g"), AX_X, ALU.add))
            step(dve.tensor_reduce(m1, sel, AX_X, ALU.max))
            first_max(hot[0], sel, m1, s[21], EG)
            step(dve.scalar_tensor_tensor(sel2, hot[0], -1e30, sel, ALU.mult, ALU.add))
            step(dve.tensor_reduce(m2, sel2, AX_X, ALU.max))
            first_max(hot[1], sel2, m2, s[21], EG)
            dve.tensor_tensor(dm, m2, m1, ALU.subtract).then_inc(rt_in, 1)
            for k in range(2):
                for g in range(G):
                    last = dve.tensor_tensor(m_k[k][:, :, g * EG:(g + 1) * EG], hot[k],
                                             hot_g[:, :, g:g + 1].broadcast_to([P, NT, EG]), ALU.mult)
            step(last)
            dve.tensor_tensor(msum[:], m_k[0][:], m_k[1][:], ALU.add).then_inc(ms_rdy, 1)
            dve.wait_ge(rt_exp, 2)
            step(dve.tensor_reduce(gsum, rt_a[:, :, 8:8 + G], AX_X, ALU.add))
            step(dve.reciprocal(gp, gsum))
            step(dve.tensor_scalar(one_ed, ed, 1.0, None, ALU.add))
            step(dve.reciprocal(r_ed, one_ed))
            step(dve.tensor_tensor(gates[:, 0, :], gp, r_ed, ALU.mult))
            step(dve.tensor_tensor(gates[:, 1, :], gates[:, 0, :], ed, ALU.mult))
            step(dve.memset(tots[:, 0, :], 0.0))
            dve.wait_ge(rank_ps, 1)
            for t in range(NT):
                step(dve.tensor_tensor(tots[:, t + 1, :], ps[:, 1, t * NE:(t + 1) * NE], tots[:, t, :], ALU.add))
            step(dve.tensor_tensor(rank[:].rearrange("p t e -> p (t e)"), ps[:, 0, 0:NT * NE],
                                   tots[:, 0:NT, :].rearrange("p t e -> p (t e)"), ALU.add))
            n_ov, n_ov2, incl, excl = (evec[:, i, :] for i in range(4))
            cnt = tots[:, NT, :]
            step(dve.tensor_scalar(n_ov, cnt, float(CAP), None, ALU.is_gt))
            for c in range(2, NC):
                step(dve.scalar_tensor_tensor(n_ov2, cnt, float(c * CAP), n_ov, ALU.is_gt, ALU.add))
                n_ov, n_ov2 = n_ov2, n_ov
            step(dve.tensor_tensor_scan(incl, ones[:, 0:NE], n_ov, 0.0, ALU.mult, ALU.add))
            step(dve.tensor_tensor(excl, incl, n_ov, ALU.subtract))
            for k in range(2):
                for dst, v in ((rk[k], rank[:]), (ek[k], over(iotaE[:], [NT, NE], 1)), (obk[k], over(excl, [NT, NE], 1))):
                    step(dve.tensor_tensor(rt_a[:], m_k[k][:], v, ALU.mult))
                    step(dve.tensor_reduce(dst, rt_a[:], AX_X, ALU.add))
                step(dve.tensor_scalar(ck[0], rk[k], float(CAP), None, ALU.is_ge))
                a, b = ck
                for c in range(2, NC):
                    step(dve.scalar_tensor_tensor(b, rk[k], float(c * CAP), a, ALU.is_ge, ALU.add))
                    a, b = b, a
                step(dve.scalar_tensor_tensor(rr[k], a, -float(CAP), rk[k], ALU.mult, ALU.add))
                step(dve.tensor_tensor(tc[k], obk[k], a, ALU.add))
                step(dve.scalar_tensor_tensor(tc[k], tc[k], float(NE - 1), ek[k], ALU.add, ALU.subtract))
                step(dve.tensor_scalar(b, a, 1.0, None, ALU.min))
                step(dve.tensor_tensor(tc[k], tc[k], b, ALU.mult))
                step(dve.tensor_tensor(tc[k], tc[k], ek[k], ALU.add))
            n = 0
            for k in range(2):
                for t in range(NT):
                    if n >= 2:
                        dve.wait_ge(oh_used, n - 1)
                    dve.tensor_scalar(oneR[:, n % 2, :], iotaR[:], rr[k][:, t:t + 1], None, ALU.is_equal)
                    for w in range(2):
                        last = dve.tensor_scalar(jcol[:, n % 2, w, :], iotaT[:], tc[k][:, t:t + 1],
                                                 tokid[:, w, k, t:t + 1], ALU.is_equal, ALU.mult)
                    last.then_inc(oh_rdy, 1)
                    n += 1
            step(dve.tensor_tensor(ovm[:], over(incl, [OV_MAX, NE], 1), over(iotaO[:], [OV_MAX, NE], 2), ALU.is_le))
            step(dve.tensor_reduce(ovn[:], ovm[:], AX_X, ALU.add))
            dve.tensor_scalar(ov_info[:, 0:OV_MAX], ovn[:], float(NE - 1), None, ALU.min)
            dve.tensor_copy(ov_info[:, OV_MAX:OV_MAX + 1], incl[:, NE - 1:NE])
            dve.wait_ge(oh_used, 2 * NT)
            dve.tensor_scalar(idx_g[0:CAP, :], ps[0:CAP, 2, 0:TILES], float(A), None, ALU.add)
            dve.tensor_scalar(idx_s[0:CAP, :], ps[0:CAP, 2, TILES:2 * TILES], float(2 * A), None, ALU.add)\
                .then_inc(idx_rdy, 1)
            dve.wait_ge(rt_exp, 2)
            dve.wait_ge(idx_rdy, 1)
            dve.memset(xg[:], 0.0).then_inc(idx_rdy, 2)

            def split_lo(e, i, b):
                k = 6 * e + i
                dve.wait_ge(hi_rdy, k + 1)
                s = (6 * b + i) % RS
                dve.tensor_tensor(w_lo[:, s, :], raw[:, i, :], w_hi[:, s, :].bitcast(F32), ALU.subtract)\
                    .then_inc(lo_rdy, 1)

            def x_lo(e):
                dve.wait_ge(xh_rdy, e + 1)
                dve.tensor_tensor(xm_lo[:].rearrange("p j i -> p (j i)"), wide(2),
                                  xm_hi[:].rearrange("p j i -> p (j i)").bitcast(F32), ALU.subtract)\
                    .then_inc(xl_rdy, 1)

            def start(e, b):
                for i in range(4):
                    split_lo(e, i, b)
                x_lo(e)

            def tile(e, b, more):
                split_lo(e, 4, b)
                split_lo(e, 5, b)
                dve.wait_ge(sg_rdy, e + 1)
                dve.wait_ge(split_used, 6 * e + 4)
                dve.tensor_tensor(hm[:].rearrange("p (j q) -> p j q", j=FC),
                                  sg[:].rearrange("p (q j) -> p j q", j=FC),
                                  ps[:, 1, :].rearrange("p (q j) -> p j q", j=FC), ALU.mult).then_inc(hm_rdy, 1)
                dve.wait_ge(hh_rdy, e + 1)
                dve.tensor_tensor(hm_lo[:].rearrange("p j i -> p (j i)"), ps[:, 4, :],
                                  hm_hi[:].rearrange("p j i -> p (j i)").bitcast(F32), ALU.subtract)\
                    .then_inc(hl_rdy, 1)
                if more:
                    x_lo(e + 1)
                    split_lo(e + 1, 0, 1 - b)
                    split_lo(e + 1, 1, 1 - b)
                dve.wait_ge(split_used, 6 * e + 6)
                if not (isinstance(e, int) and e == 0):
                    dve.wait_ge(y_out, 16 * e)
                dve.tensor_copy(ym[:, 512:D], ps[:, 6, :]).then_inc(yd_rdy, 1)
                if more:
                    split_lo(e + 1, 2, 1 - b)
                    split_lo(e + 1, 3, 1 - b)

            work_off_tiles(dve, start, tile)
            for t in range(NT + 1):
                if t < NT:
                    dve.wait_ge(yk_in[t % 2], 32 * (t // 2 + 1))
                    v = x2[:, t, :]
                    dve.scalar_tensor_tensor(v, yk[:, t % 2, 0, :], gates[:, 0, t:t + 1], v, ALU.mult, ALU.add)\
                        .then_inc(y0_rdy, 1)
                    dve.wait_ge(y0_rdy, t + 1)
                    dve.scalar_tensor_tensor(v, yk[:, t % 2, 1, :], gates[:, 1, t:t + 1], v, ALU.mult, ALU.add)\
                        .then_inc(x3_rdy, 1)
                if t:
                    u = t - 1
                    dve.wait_ge(x3_rdy, u + 1)
                    dve.wait_ge(r3_rdy, u + 1)
                    if u >= 2:
                        dve.wait_ge(out_done[u % 2], 16 * (u // 2))
                    dve.scalar_tensor_tensor(fin[:, u % 2, :], x2[:, u, :], stat[:, 56 + u:57 + u], g_fin[:],
                                             ALU.mult, ALU.mult).then_inc(fin_rdy, 1)

        @block.tensor
        def _(pe):
            pe.wait_ge(const_rdy, 2)
            pe.wait_ge(rows_in, 16 * 6)
            pe.transpose(ps[:, 0, 0:22], prow[:], ident[0:22, 0:22])
            for c in range(CT):
                last = pe.transpose(ps[:, 0, 22 + c * TAPS:22 + (c + 1) * TAPS], cwrow[:, c * P:(c + 1) * P],
                                    ident[0:TAPS, 0:TAPS])
            last.then_inc(pcol_ps, 1)
            for i in range(NT):
                pe.wait_ge(xs_rdy, i + 1)
                if i >= 2:
                    pe.wait_ge(xn_rdy, i - 1)
                for k in range(KC):
                    last = pe.transpose(wide(4 + 2 * (i % 2))[:, k * P:(k + 1) * P], xa[:, i % XS, k * P:(k + 1) * P],
                                        ident[:])
                last.then_inc(tr_ps, 1)
            pe.wait_ge(low_in, 32)

            def piece(n):
                return raw[:, n % RW, :].rearrange("p (j n) -> p j n", n=256)

            for n, (what, c, h) in enumerate(groups):
                if n >= 4:
                    pe.wait_ge(*evacuated(n - 4))
                cols = slice(h * 512, (h + 1) * 512)
                m = RANK if what == "low" else P
                dst = ps[0:m, n % 4, :]
                if n < HALF:
                    pe.wait_ge(xn_rdy, (h + 1) * NT // HALF)
                    if n == 0:
                        pe.wait_ge(pcol_rdy, 1)
                if what == "gk":
                    pe.wait_ge(tg_act, HALF)
                    pe.matmul(dst, gkw[:, c * P:(c + 1) * P], lowT[:, cols], start=True, stop=True).then_inc(tg_ps, 1)
                    continue
                if what == "low":
                    w = w_low[:]
                else:
                    q = piece_of[what, c // 2 if what in ("gate", "a") else 0]
                    pe.wait_ge(raw_in[q % RW], 16 * (q // RW + 1))
                    w = piece(q)[:, :, (c % 2) * P:(c % 2 + 1) * P]
                for k in range(KC):
                    last = pe.matmul(dst, w[:, k, :], xnT[:, k, cols], start=(k == 0), stop=(k == KC - 1))
                last.then_inc(tg_ps, 1)
                if what != "low" and c % 2 == 1 and h == HALF - 1:
                    pe.wait_ge(tg_ps, n + 1)
                    pe.sem_inc(w_used, 1)

            def project(t, q, b, done, free, n_free):
                if n_free:
                    pe.wait_ge(free, n_free)
                for i in range(2):
                    pe.wait_ge(raw_in[(q + i) % RW], 16 * ((q + i) // RW + 1))
                    for k in range(KC):
                        last = pe.matmul(ps[:, b, i * 256:(i + 1) * 256], xnT[:, k, t * P:(t + 1) * P],
                                         piece(q + i)[:, k, :], start=(k == 0), stop=(k == KC - 1))
                last.then_inc(done, 1)

            pe.wait_ge(tg_dve, N_DVE)
            pe.wait_ge(tg_act, N_ACT)
            project(0, 6, 0, v_ps, v_rdy, 0)
            project(0, 8, 1, g_ps, g_rdy, 0)
            pe.wait_ge(const_rdy, 8)

            def gla_transpose(t):
                pe.wait_ge(gl_rdy, t + 1)
                if t:
                    pe.wait_ge(gla_rdy, t)
                for h in range(HEADS):
                    last = pe.transpose(ps[:, 7, h * P:(h + 1) * P], gl[:, h * HV:(h + 1) * HV], ident[:])
                last.then_inc(gt_ps, 1)

            for t in range(NT):
                tok = slice(t * P, (t + 1) * P)
                pe.wait_ge(ks_rdy, t + 1)
                if t:
                    pe.wait_ge(kz_rdy, t)
                for pr in range(PAIRS):
                    last = pe.transpose(ps[:, 6, pr * P:(pr + 1) * P], ksT[:, pr, :], ident[:])
                last.then_inc(kt_ps, 1)
                if t:
                    pe.wait_ge(ssb_rdy, t)
                for pr in range(PAIRS):
                    last = pe.matmul(ps[:, 3, pr * 2 * P:(pr + 1) * 2 * P].rearrange("p (h i) -> p h i", h=2),
                                     kT[:, pr, tok], qz[:, 2 * pr:2 * pr + 2, tok], start=True, stop=True)
                last.then_inc(s_ps, 1)
                if t + 1 < NT:
                    project(t + 1, 6, 0, v_ps, v_rdy, t + 1)
                if t:
                    gla_transpose(t - 1)
                pe.wait_ge(kz_rdy, t + 1)
                pe.wait_ge(v_rdy, t + 1)
                if t:
                    pe.wait_ge(st_rdy, 2 * t)
                for c in range(2):
                    for pr in range(PAIRS):
                        cols = slice(pr * 2 * HV, (pr + 1) * 2 * HV)
                        last = pe.matmul(ps[:, 4 + c, cols], kz[:, c, pr * P:(pr + 1) * P], vt[:, t % 2, cols],
                                         start=True, stop=True)
                last.then_inc(kv_ps, 1)
                if t + 1 < NT:
                    project(t + 1, 8, 1, g_ps, g_rdy, t + 1)
                pe.wait_ge(ssb_rdy, t + 1)
                pe.wait_ge(st_rdy, 2 * t + 1)
                if t:
                    pe.wait_ge(gl_rdy, t)
                for h in range(HEADS):
                    cols = slice(h * HV, (h + 1) * HV)
                    pe.matmul(ps[:, 2, cols], ssb[:, t % 2, h * P:(h + 1) * P], vt[:, t % 2, cols],
                              start=True, stop=False, skip_group_check=True)
                    for c in range(2):
                        last = pe.matmul(ps[c * CH:(c + 1) * CH, 2, cols],
                                         qz[:, h, t * P + c * CH:t * P + (c + 1) * CH],
                                         st[:, (2 * t + c) % 4, h // 2, (h % 2) * HV:(h % 2 + 1) * HV],
                                         start=False, stop=True, skip_group_check=True)
                last.then_inc(o_ps, 1)
            pe.wait_ge(o_ps, NT)
            pe.sem_inc(w_used, 4)
            gla_transpose(NT - 1)
            pe.wait_ge(conv_step, CT * TAPS)
            pe.wait_ge(v_rdy, NT)
            pe.wait_ge(g_rdy, NT)

            def channel_mean(src, ready, b, done):
                for h in range(HALF):
                    if ready is not None:
                        pe.wait_ge(ready, h + 1)
                    for c in range(CT):
                        last = pe.matmul(ps[:, b + h, :], ones_dc[:], src[:, c, h * 512:(h + 1) * 512],
                                         start=(c == 0), stop=(c == CT - 1))
                    last.then_inc(done, 1)

            channel_mean(acc, None, 0, mu_ps)
            pe.wait_ge(gl_rdy, NT)
            pe.wait_ge(ssb_rdy, NT)
            channel_mean(sq, sq_rdy, 2, var_ps)

            def out_projection(t, half):
                if t == 0:
                    pe.wait_ge(d_rdy, HALF)
                if t == 1:
                    pe.wait_ge(sd_rdy, HALF)
                if t >= 2:
                    pe.wait_ge(x2_rdy, t - 1)
                for i in (0, 1) if half == 0 else (2, 3):
                    n = N_IN + i
                    pe.wait_ge(raw_in[n % RW], 16 * (n // RW + 1))
                    for k in range(KC):
                        src = acc[:, k, :] if k < CT else glaT[:, k - CT, :]
                        last = pe.matmul(wide(2 * (t % 2))[:, i * 256:(i + 1) * 256], src[:, t * P:(t + 1) * P],
                                         piece(n)[:, k, :], start=(k == 0), stop=(k == KC - 1))
                if half:
                    last.then_inc(yo_ps, 1)

            pe.wait_ge(c_rdy, CT * HALF)
            pe.wait_ge(gla_rdy, NT)
            pe.wait_ge(st_rdy, 2 * NT)
            def logits_transposed(t):
                pe.wait_ge(lgT_rdy, t + 1)
                pe.transpose(ps[:, 7, t * NR:(t + 1) * NR], logT[:, t * P:(t + 1) * P], ident[0:NR, 0:NR])\
                    .then_inc(lt_ps, 1)

            out_projection(0, 0)
            out_projection(0, 1)
            for t in range(NT):
                if t + 1 < NT:
                    out_projection(t + 1, 0)
                if t:
                    logits_transposed(t - 1)
                    pe.wait_ge(hfT_rdy, t)
                pe.wait_ge(hf_rdy, t + 1)
                for k in range(KC):
                    last = pe.transpose(wide(4)[:, k * P:(k + 1) * P], hfp[:, t % 2, k * P:(k + 1) * P], ident[:])
                last.then_inc(th_ps, 1)
                if t + 1 < NT:
                    out_projection(t + 1, 1)
                if t == NT - 2:
                    pe.wait_ge(yo_ps, NT)
                    pe.sem_inc(w_used, 4)
                pe.wait_ge(hfT_rdy, t + 1)
                for k in range(KC):
                    last = pe.matmul(ps[0:NR, 6, 0:P], r_w[:, k, :], hfT[:, k, :], start=(k == 0), stop=(k == KC - 1))
                last.then_inc(lg_ps, 1)
            logits_transposed(NT - 1)
            pe.wait_ge(const_rdy, 11)
            pe.wait_ge(ms_rdy, 1)
            pe.wait_ge(x2_rdy, NT)
            v = msum[:].rearrange("p t e -> p (t e)")
            pe.matmul(ps[:, 0, 0:NT * NE], upper[:], v, start=True, stop=True)
            pe.matmul(ps[:, 1, 0:NT * NE], ones[:], v, start=True, stop=True).then_inc(rank_ps, 1)
            for n in range(2 * NT):
                pe.wait_ge(oh_rdy, n + 1)
                pe.matmul(ps[0:CAP, 2, 0:2 * TILES], oneR[:, n % 2, :], jcol[:, n % 2, :, :].rearrange("p w t -> p (w t)"),
                          start=(n == 0), stop=(n == 2 * NT - 1)).then_inc(oh_used, 1)
            pe.wait_ge(idx_rdy, 1)

            def rows_transposed(e, b):
                pe.wait_ge(g_in, 16 * e + 16)
                for k in range(KC):
                    last = pe.transpose(wide(2)[:, k * P:(k + 1) * P], xg[:, k * P:(k + 1) * P], ident[:])
                last.then_inc(xgt_ps, 1)

            def split_product(dst, x_hi, x_lo, s, cols, first, stop):
                pe.matmul(dst, x_hi, w_hi[:, s, cols], start=first, stop=False)
                pe.matmul(dst, x_hi, w_lo[:, s, cols], start=False, stop=False)
                return pe.matmul(dst, x_lo, w_hi[:, s, cols], start=False, stop=stop)

            def tile(e, b, more):
                pe.wait_ge(xl_rdy, e + 1)
                for i in range(4):
                    pe.wait_ge(lo_rdy, 6 * e + i + 1)
                    for k in range(4):
                        kk = 4 * (i % 2) + k
                        last = split_product(ps[:, i // 2, :], xm_hi[:, kk, :], xm_lo[:, kk, :], (6 * b + i) % RS,
                                             slice(k * F, (k + 1) * F), kk == 0, kk == KC - 1)
                    last.then_inc(split_used, 1)
                    if more and i == 1:
                        rows_transposed(e + 1, 1 - b)
                pe.wait_ge(hm_rdy, e + 1)
                for k in range(FC):
                    last = pe.transpose(ps[:, 4, k * P:(k + 1) * P], hm[:, k * P:(k + 1) * P], ident[:])
                last.then_inc(ht_ps, 1)
                pe.wait_ge(hl_rdy, e + 1)
                if not (isinstance(e, int) and e == 0):
                    pe.wait_ge(ya_rdy, e)
                    pe.wait_ge(yd_rdy, e)
                for i in range(2):
                    pe.wait_ge(lo_rdy, 6 * e + 5 + i)
                    for k in range(2):
                        kk = 2 * i + k
                        for n in range(2):
                            last = split_product(ps[:, 5 + n, :], hm_hi[:, kk, :], hm_lo[:, kk, :],
                                                 (6 * b + 4 + i) % RS, slice(k * D + n * 512, k * D + (n + 1) * 512),
                                                 kk == 0, kk == FC - 1)
                    last.then_inc(split_used, 1)

            work_off_tiles(pe, rows_transposed, tile)


_INS = ['x', 'attn_norm_g', 'w_in', 'conv_w', 'conv_b', 'conv_ln_g', 'conv_ln_b', 'gk_w', 'gk_b', 'gla_norm_g',
        'w_out', 'ffn_norm_g', 'router_group_w', 'router_group_b', 'router_expert_w', 'router_expert_b',
        'expert_w_gate', 'expert_w_up', 'expert_w_down', 'final_norm_g']
_OUTS = [((1, 1024, 1024), 'float32')]


def kernel(**inputs):
    import numpy as _np
    import concourse.bacc as _bacc
    from concourse import mybir as _mybir
    from concourse.bass_utils import run_bass_kernel_spmd as _run

    nc = _bacc.Bacc("TRN2", target_bir_lowering=False, num_devices=1)
    arrays, args = {}, []
    for name in _INS:
        a = _np.ascontiguousarray(inputs[name])
        arrays[f"in_{name}_dram"] = a
        args.append(nc.dram_tensor(f"in_{name}_dram", a.shape, _mybir.dt.from_np(a.dtype), kind="ExternalInput").ap())
    for i, (shape, dtype) in enumerate(_OUTS):
        dt = _mybir.dt.from_np(_np.dtype(dtype))
        args.append(nc.dram_tensor(f"out_{i}_dram", shape, dt, kind="ExternalOutput").ap())
    layer_program(nc, *args)
    r = _run(nc, [arrays], core_ids=[0])
    return r.results[0]["out_0_dram"]
```
